# Optimizing a Trainium2 kernel written in Bass

```python
import math
import jax, jax.numpy as jnp
from jax import lax
import numpy as np

D_MODEL = 2048
BATCH = 1
SEQ = 512
DEPTH = 1

N_MIXERS = 3
D_INNER = D_MODEL
DIFF_HEADS = 8
DIFF_QK_DIM = D_INNER // (2 * DIFF_HEADS)
DIFF_V_DIM = 2 * DIFF_QK_DIM
MOBA_HEADS = 16
MOBA_HEAD_DIM = D_INNER // MOBA_HEADS
MOBA_BLOCK = 256
MOBA_TOPK = 3
MOBA_Q_CHUNK = 32
FOX_HEADS = 16
FOX_HEAD_DIM = D_INNER // FOX_HEADS
FORGET_W_SCALE = 0.1
FORGET_B_MIN = 2.0
FORGET_B_MAX = 5.0
REL_BUCKETS = 32
REL_MAX_DIST = 128
REL_HEADS = 16
Q_BLOCK = 128
LN_EPS = 1e-5
RMS_EPS = 1e-5
NEG = -1e30
DN_ALPHA = (2.0 * DEPTH) ** 0.25
DN_BETA = (8.0 * DEPTH) ** -0.25

kernel_name = "hybrid_diff_moba_fox_deepnorm"

def layer_norm(x, g, b):
    xf = x.astype(jnp.float32)
    mu = jnp.mean(xf, axis=-1, keepdims=True)
    var = jnp.mean(jnp.square(xf - mu), axis=-1, keepdims=True)
    return ((xf - mu) * lax.rsqrt(var + LN_EPS) * g + b).astype(x.dtype)

def rms_norm(x, g):
    xf = x.astype(jnp.float32)
    return (xf * lax.rsqrt(jnp.mean(jnp.square(xf), axis=-1, keepdims=True) + RMS_EPS) * g).astype(x.dtype)

def t5_bucket(dist):
    n = jnp.maximum(dist, 0)
    max_exact = REL_BUCKETS // 2
    nf = jnp.maximum(n, 1).astype(jnp.float32)
    large = max_exact + (jnp.log(nf / max_exact) / math.log(REL_MAX_DIST / max_exact)
                         * (REL_BUCKETS - max_exact)).astype(jnp.int32)
    large = jnp.minimum(large, REL_BUCKETS - 1)
    return jnp.where(n < max_exact, n, large)

def rel_bias_dense(table, q_pos, k_pos):
    return jnp.moveaxis(table[t5_bucket(q_pos[:, None] - k_pos[None, :])], -1, 0).astype(jnp.float32)

def split_heads(t, n_heads):
    B, S, _ = t.shape
    return t.reshape(B, S, n_heads, -1).transpose(0, 2, 1, 3)

def merge_blocks(o):
    nb, B, H, Qb, d = o.shape
    return o.transpose(1, 0, 3, 2, 4).reshape(B, nb * Qb, H * d)

def diff_attention(u, w_in, w_out, lam_q1, lam_k1, lam_q2, lam_k2, subln_g, rel_table, layer_idx):
    B, S, _ = u.shape
    E = D_INNER
    proj = u @ w_in
    q = split_heads(proj[..., :E], 2 * DIFF_HEADS)
    k = split_heads(proj[..., E:2 * E], 2 * DIFF_HEADS)
    v = split_heads(proj[..., 2 * E:3 * E], DIFF_HEADS)
    z = proj[..., 3 * E:4 * E]
    lam_init = 0.8 - 0.6 * math.exp(-0.3 * layer_idx)
    lam = (jnp.exp(jnp.sum((lam_q1 * lam_k1).astype(jnp.float32)))
           - jnp.exp(jnp.sum((lam_q2 * lam_k2).astype(jnp.float32))) + lam_init)
    scale = DIFF_QK_DIM ** -0.5
    nb = S // Q_BLOCK
    k_pos = jnp.arange(S)
    q_blocks = q.reshape(B, 2 * DIFF_HEADS, nb, Q_BLOCK, DIFF_QK_DIM).transpose(2, 0, 1, 3, 4)

    def block(args):
        q_blk, start = args
        q_pos = start + jnp.arange(Q_BLOCK)
        logits = (jnp.einsum('bhqd,bhsd->bhqs', q_blk, k).astype(jnp.float32) * scale
                  + rel_bias_dense(rel_table, q_pos, k_pos)[None])
        logits = jnp.where(k_pos[None, :] <= q_pos[:, None], logits, NEG)
        p = jax.nn.softmax(logits, axis=-1).reshape(B, DIFF_HEADS, 2, Q_BLOCK, S)
        a = p[:, :, 0] - lam * p[:, :, 1]
        return jnp.einsum('bhqs,bhsd->bhqd', a.astype(v.dtype), v)

    o = lax.map(block, (q_blocks, jnp.arange(nb) * Q_BLOCK))
    o = rms_norm(o, subln_g) * (1.0 - lam_init)
    o = merge_blocks(o)
    return (o * jax.nn.silu(z)) @ w_out

def moba_attention(u, w_in, w_out, rel_table):
    B, S, _ = u.shape
    E, H, d = D_INNER, MOBA_HEADS, MOBA_HEAD_DIM
    proj = u @ w_in
    q = split_heads(proj[..., :E], H)
    k = split_heads(proj[..., E:2 * E], H)
    v = split_heads(proj[..., 2 * E:3 * E], H)
    z = proj[..., 3 * E:4 * E]
    n_kb = -(-S // MOBA_BLOCK)
    pad = n_kb * MOBA_BLOCK - S
    k_blocks = jnp.pad(k, ((0, 0), (0, 0), (0, pad), (0, 0))).reshape(B, H, n_kb, MOBA_BLOCK, d)
    v_blocks = jnp.pad(v, ((0, 0), (0, 0), (0, pad), (0, 0))).reshape(B, H, n_kb, MOBA_BLOCK, d)
    k_mean = jnp.mean(k_blocks.astype(jnp.float32), axis=3)
    top_k = max(1, min(MOBA_TOPK, n_kb - 1))
    scale = d ** -0.5
    bi = jnp.arange(B)[:, None, None, None]
    hi = jnp.arange(H)[None, :, None, None]
    hi5 = jnp.arange(H)[None, :, None, None, None]
    n_chunks = S // MOBA_Q_CHUNK
    q_chunks = q.reshape(B, H, n_chunks, MOBA_Q_CHUNK, d).transpose(2, 0, 1, 3, 4)
    blk_off = jnp.arange(MOBA_BLOCK)

    def chunk(args):
        q_blk, start = args
        q_pos = start + jnp.arange(MOBA_Q_CHUNK)
        own = start // MOBA_BLOCK
        gate = jnp.einsum('bhqd,bhnd->bhqn', q_blk.astype(jnp.float32), k_mean)
        gate = jnp.where(jnp.arange(n_kb) < own, gate, NEG)
        _, sel = lax.top_k(gate, top_k)
        sel_valid = sel < own
        k_sel = k_blocks[bi, hi, sel]
        v_sel = v_blocks[bi, hi, sel]
        sel_pos = sel[..., None] * MOBA_BLOCK + blk_off
        logit_sel = jnp.einsum('bhqd,bhqkcd->bhqkc', q_blk, k_sel).astype(jnp.float32) * scale
        logit_sel = logit_sel + rel_table[t5_bucket(q_pos[None, None, :, None, None] - sel_pos), hi5].astype(jnp.float32)
        logit_sel = jnp.where(sel_valid[..., None], logit_sel, NEG)
        k_own = lax.dynamic_index_in_dim(k_blocks, own, axis=2, keepdims=False)
        v_own = lax.dynamic_index_in_dim(v_blocks, own, axis=2, keepdims=False)
        own_pos = own * MOBA_BLOCK + blk_off
        logit_own = (jnp.einsum('bhqd,bhcd->bhqc', q_blk, k_own).astype(jnp.float32) * scale
                     + rel_bias_dense(rel_table, q_pos, own_pos)[None])
        logit_own = jnp.where(own_pos[None, :] <= q_pos[:, None], logit_own, NEG)
        n_sel = top_k * MOBA_BLOCK
        logits = jnp.concatenate([logit_sel.reshape(B, H, MOBA_Q_CHUNK, n_sel), logit_own], axis=-1)
        p = jax.nn.softmax(logits, axis=-1)
        p_sel = p[..., :n_sel].reshape(B, H, MOBA_Q_CHUNK, top_k, MOBA_BLOCK).astype(v.dtype)
        p_own = p[..., n_sel:].astype(v.dtype)
        return (jnp.einsum('bhqkc,bhqkcd->bhqd', p_sel, v_sel)
                + jnp.einsum('bhqc,bhcd->bhqd', p_own, v_own))

    o = merge_blocks(lax.map(chunk, (q_chunks, jnp.arange(n_chunks) * MOBA_Q_CHUNK)))
    return (o * jax.nn.silu(z)) @ w_out

def forgetting_attention(u, w_in, w_out, b_f):
    B, S, _ = u.shape
    E, H, d = D_INNER, FOX_HEADS, FOX_HEAD_DIM
    proj = u @ w_in
    q = split_heads(proj[..., :E], H)
    k = split_heads(proj[..., E:2 * E], H)
    v = split_heads(proj[..., 2 * E:3 * E], H)
    z = proj[..., 3 * E:4 * E]
    log_f = jax.nn.log_sigmoid((proj[..., 4 * E:] + b_f).astype(jnp.float32))
    cum = jnp.cumsum(log_f, axis=1).transpose(0, 2, 1)
    scale = d ** -0.5
    nb = S // Q_BLOCK
    k_pos = jnp.arange(S)
    q_blocks = q.reshape(B, H, nb, Q_BLOCK, d).transpose(2, 0, 1, 3, 4)
    c_blocks = cum.reshape(B, H, nb, Q_BLOCK).transpose(2, 0, 1, 3)

    def block(args):
        q_blk, c_blk, start = args
        q_pos = start + jnp.arange(Q_BLOCK)
        logits = (jnp.einsum('bhqd,bhsd->bhqs', q_blk, k).astype(jnp.float32) * scale
                  + c_blk[..., :, None] - cum[..., None, :])
        logits = jnp.where(k_pos[None, :] <= q_pos[:, None], logits, NEG)
        p = jax.nn.softmax(logits, axis=-1)
        return jnp.einsum('bhqs,bhsd->bhqd', p.astype(v.dtype), v)

    o = merge_blocks(lax.map(block, (q_blocks, c_blocks, jnp.arange(nb) * Q_BLOCK)))
    return (o * jax.nn.silu(z)) @ w_out

def setup_inputs(seed: int = 0) -> dict:
    key = jax.random.key(seed)
    ks = iter(jax.random.split(key, 32))
    f32 = jnp.float32
    s_in = D_MODEL ** -0.5

    def in_proj(k, extra_cols=0):
        scales = jnp.concatenate([
            jnp.full((2 * D_INNER,), s_in, f32),
            jnp.full((D_INNER,), DN_BETA * s_in, f32),
            jnp.full((D_INNER,), s_in, f32),
            jnp.full((extra_cols,), FORGET_W_SCALE * s_in, f32)])
        return jax.random.normal(k, (D_MODEL, 4 * D_INNER + extra_cols), f32) * scales

    def out_proj(k):
        return jax.random.normal(k, (D_INNER, D_MODEL), f32) * (DN_BETA * D_INNER ** -0.5)

    def gain(k, n):
        return 1.0 + 0.02 * jax.random.normal(k, (n,), f32)

    def small(k, n, s=0.02):
        return s * jax.random.normal(k, (n,), f32)

    p = {}
    p["x"] = jax.random.normal(next(ks), (BATCH, SEQ, D_MODEL), f32)
    p["rel_bias"] = 0.5 * jax.random.normal(next(ks), (REL_BUCKETS, REL_HEADS), f32)
    for i in (0,):
        pass
    p["w_in_0"] = in_proj(next(ks))
    p["lam_q1_0"] = small(next(ks), DIFF_QK_DIM, 0.1)
    p["lam_k1_0"] = small(next(ks), DIFF_QK_DIM, 0.1)
    p["lam_q2_0"] = small(next(ks), DIFF_QK_DIM, 0.1)
    p["lam_k2_0"] = small(next(ks), DIFF_QK_DIM, 0.1)
    p["subln_g_0"] = gain(next(ks), DIFF_V_DIM)
    p["w_out_0"] = out_proj(next(ks))
    p["ln_g_0"] = gain(next(ks), D_MODEL)
    p["ln_b_0"] = small(next(ks), D_MODEL)
    p["w_in_1"] = in_proj(next(ks))
    p["w_out_1"] = out_proj(next(ks))
    p["ln_g_1"] = gain(next(ks), D_MODEL)
    p["ln_b_1"] = small(next(ks), D_MODEL)
    p["w_in_2"] = in_proj(next(ks), FOX_HEADS)
    p["b_f_2"] = jax.random.uniform(next(ks), (FOX_HEADS,), f32, FORGET_B_MIN, FORGET_B_MAX)
    p["w_out_2"] = out_proj(next(ks))
    p["ln_g_2"] = gain(next(ks), D_MODEL)
    p["ln_b_2"] = small(next(ks), D_MODEL)
    p["w_in_3"] = in_proj(next(ks))
    p["lam_q1_3"] = small(next(ks), DIFF_QK_DIM, 0.1)
    p["lam_k1_3"] = small(next(ks), DIFF_QK_DIM, 0.1)
    p["lam_q2_3"] = small(next(ks), DIFF_QK_DIM, 0.1)
    p["lam_k2_3"] = small(next(ks), DIFF_QK_DIM, 0.1)
    p["subln_g_3"] = gain(next(ks), DIFF_V_DIM)
    p["w_out_3"] = out_proj(next(ks))
    p["ln_g_3"] = gain(next(ks), D_MODEL)
    p["ln_b_3"] = small(next(ks), D_MODEL)
    return p

def reference(x, rel_bias,
              w_in_0, lam_q1_0, lam_k1_0, lam_q2_0, lam_k2_0, subln_g_0, w_out_0, ln_g_0, ln_b_0,
              w_in_1, w_out_1, ln_g_1, ln_b_1,
              w_in_2, b_f_2, w_out_2, ln_g_2, ln_b_2,
              w_in_3, lam_q1_3, lam_k1_3, lam_q2_3, lam_k2_3, subln_g_3, w_out_3, ln_g_3, ln_b_3):
    layers = [
        (w_in_0, w_out_0, (lam_q1_0, lam_k1_0, lam_q2_0, lam_k2_0, subln_g_0), ln_g_0, ln_b_0),
        (w_in_1, w_out_1, (), ln_g_1, ln_b_1),
        (w_in_2, w_out_2, (b_f_2,), ln_g_2, ln_b_2),
        (w_in_3, w_out_3, (lam_q1_3, lam_k1_3, lam_q2_3, lam_k2_3, subln_g_3), ln_g_3, ln_b_3),
    ]
    h = x
    for i in range(DEPTH):
        w_in, w_out, extra, g, b = layers[i]
        kind = i % N_MIXERS
        if kind == 0:
            y = diff_attention(h, w_in, w_out, *extra, rel_bias, i)
        elif kind == 1:
            y = moba_attention(h, w_in, w_out, rel_bias)
        else:
            y = forgetting_attention(h, w_in, w_out, *extra)
        h = layer_norm(DN_ALPHA * h + y, g, b)
    return h


_drawn_inputs = setup_inputs


def setup_inputs(seed=0):
    import zlib

    import numpy as np

    out = dict(_drawn_inputs(seed))
    spreads = {}
    factors = {'lam_q1_0': 6.441,
     'lam_k1_0': 4.185,
     'subln_g_0': 71.071,
     'ln_g_0': 21.63,
     'ln_b_0': 22.21,
     'lam_q2_0': 64.0,
     'lam_k2_0': 8.0}
    for name, (base, spread) in spreads.items():
        noise = np.random.default_rng([zlib.crc32(name.encode()), seed]).standard_normal(out[name].shape)
        drawn = base * np.exp(spread * noise) if base else spread * noise
        out[name] = __import__('jax').numpy.asarray(drawn.astype(out[name].dtype))
    for name, factor in factors.items():
        out[name] = (out[name] * factor).astype(out[name].dtype)
    return out
```

```python
from contextlib import ExitStack
import math

import concourse.bass as bass
from concourse import mybir

ALU = mybir.AluOpType
ACT = mybir.ActivationFunctionType
F32 = mybir.dt.float32
F32R = mybir.dt.float32r

P = 128
SEQ = 512
D = 2048
PAIRS = 8
PW = D // PAIRS
HD = PW // 2
ST = SEQ // P
KT = D // P
QK = 4
QUARTERS = 4 * 4
QE = QK * PW
RING = 4
LEAD = RING - 1
NC = 512
CHUNKS = D // NC
OK = QE // NC
OQ = KT // OK
BUCKETS = 32
BIAS_W = 640
SCALE = float(HD) ** -0.5
LAM_INIT = 0.8 - 0.6 * math.exp(-0.3 * 0)
ALPHA = 2.0 ** 0.25
EPS = 1e-5
MASKED = -1e30
LOWEST = -3.0e38


def diff_layer(nc, x, rel_bias, w_in, lam_q1, lam_k1, lam_q2, lam_k2, subln_g, w_out, ln_g, ln_b,
               bucket_onehot, out):
    with ExitStack() as ctx:
        def sb(name, shape, dt=F32):
            return ctx.enter_context(nc.sbuf_tensor(name, shape, dt))

        def sem(name):
            return ctx.enter_context(nc.semaphore(name))

        xg_split = sb("xg_split", [P, 2, KT, SEQ], F32R)
        big = sb("big", [P, D * ST])
        x_rows = big[:].rearrange("p (s d) -> p s d", s=ST)
        g = big[:].rearrange("p (k s) -> p k s", k=KT)
        r_rows = x_rows
        w_raw = sb("w_raw", [P, RING, QE])
        w_split = sb("w_split", [P, RING, 2, QE], F32R)
        operands = sb("operands", [P, 8 * QE], F32R)
        qT = operands[:, 0:2 * QE].rearrange("p (l h s) -> p l h s", l=2, h=2)
        kT = operands[:, 2 * QE:4 * QE].rearrange("p (l h s) -> p l h s", l=2, h=2)
        v = operands[:, 4 * QE:6 * QE].rearrange("p (l t e) -> p l t e", l=2, t=ST)
        aT = operands[:, 6 * QE:8 * QE].rearrange("p (b l s) -> p b l s", b=2, l=2)
        w_late = operands[:].rearrange("p (q l e) -> p q l e", q=4, l=2)
        scratch = sb("scratch", [P, 2 * D])
        logits = scratch[:, 0:1024].rearrange("p (h s) -> p h s", h=2)
        a_rows = scratch[:, 1024:2048].rearrange("p (b s) -> p b s", b=2)
        silu_z = scratch[:, 2048:3072].rearrange("p (e s) -> p e s", e=2)
        normed = scratch[:, 3072:4096].rearrange("p (t e) -> p t e", t=ST)
        onehot = scratch[0:BUCKETS + 1, 0:BIAS_W]
        bias_line = scratch[0:16, 1024:1024 + BIAS_W]
        ln_g_all, ln_b_all = scratch[:, 0:D], scratch[:, D:2 * D]
        bias = sb("bias", [P, 2, SEQ])
        x_res = sb("x_res", [P, ST, NC])
        ident = sb("ident", [P, P])
        ones = sb("ones", [P, P])
        table = sb("table", [BUCKETS + 1, 16])
        lam_vecs = sb("lam_vecs", [P, 4])
        lam_prod = sb("lam_prod", [P, 2])
        lam_exp = sb("lam_exp", [P, 2])
        lam_diff = sb("lam_diff", [P, 1])
        neg_lam = sb("neg_lam", [P, 1])
        sub_raw = sb("sub_raw", [P, 2])
        sub_g = sb("sub_g", [P, 2])
        minus_half = sb("minus_half", [P, 1])
        row_max = sb("row_max", [P, 2])
        neg_max = sb("neg_max", [P, 2])
        row_sum = sb("row_sum", [P, 2])
        inv_sum = sb("inv_sum", [P, ST, 2])
        mix = sb("mix", [P, 1])
        sq_sum = sb("sq_sum", [P, ST])
        mean_sq = sb("mean_sq", [P, ST])
        rms = sb("rms", [P, ST])
        o_scale = sb("o_scale", [P, ST])
        stats = sb("stats", [P, ST, CHUNKS, 6])
        mean_var = sb("mean_var", [P, ST, 2])
        var_eps = sb("var_eps", [P, ST])
        r_std = sb("r_std", [P, ST])
        bias_dram = nc.dram_tensor("bias_by_distance", (16, P, BIAS_W), F32, kind="Internal")

        proj = ctx.enter_context(nc.psum_tensor("proj", [P, 4, 512], F32))
        att = ctx.enter_context(nc.psum_tensor("att", [P, 4, 512], F32))
        scores = att[:, 0:2]
        turned = att[:, 2]
        av = att[:, 3, 0:PW]

        x_loaded = [sem(f"x_loaded{i}") for i in range(4)]
        raw_loaded = [sem(f"raw_loaded{i}") for i in range(RING)]
        small_loaded = sem("small_loaded")
        sub_loaded = sem("sub_loaded")
        table_loaded = sem("table_loaded")
        bias_stored = sem("bias_stored")
        bias_loaded = sem("bias_loaded")
        res_loaded = sem("res_loaded")
        ln_loaded = sem("ln_loaded")
        out_stored = sem("out_stored")
        ident_zero = sem("ident_zero")
        consts_ready = sem("consts_ready")
        mask_ready = sem("mask_ready")
        bias_line_done = sem("bias_line_done")
        bias_line_ready = sem("bias_line_ready")
        lam_step = sem("lam_step")
        lam_sums = sem("lam_sums")
        lam_exped = sem("lam_exped")
        xT_done = sem("xT_done")
        xT_hi = sem("xT_hi")
        xT_ready = sem("xT_ready")
        w_hi = sem("w_hi")
        w_ready = sem("w_ready")
        quarter_done = sem("quarter_done")
        chunk_hi = sem("chunk_hi")
        chunk_moved = sem("chunk_moved")
        z_step = sem("z_step")
        scores_done = sem("scores_done")
        tile_begun = sem("tile_begun")
        max_ready = sem("max_ready")
        neg_max_ready = sem("neg_max_ready")
        exp_ready = sem("exp_ready")
        inv_ready = sem("inv_ready")
        mix_ready = sem("mix_ready")
        a_ready = sem("a_ready")
        aT_done = sem("aT_done")
        aT_hi = sem("aT_hi")
        aT_ready = sem("aT_ready")
        av_done = sem("av_done")
        sq_ready = sem("sq_ready")
        mean_ready = sem("mean_ready")
        rms_ready = sem("rms_ready")
        o_scale_ready = sem("o_scale_ready")
        normed_ready = sem("normed_ready")
        nT_done = sem("nT_done")
        g_ready = sem("g_ready")
        g_hi = sem("g_hi")
        g_split = sem("g_split")
        tile_done = sem("tile_done")
        r_ready = sem("r_ready")
        stats_ready = sem("stats_ready")
        mv_ready = sem("mv_ready")
        var_ready = sem("var_ready")
        r_std_ready = sem("r_std_ready")
        centred = sem("centred")
        rows_ready = sem("rows_ready")

        TOTAL = PAIRS * QUARTERS

        def ring(n):
            return n % RING

        def split_view(n_static, part):
            return w_split[:, ring(n_static), part]

        def out_split_view(n, part):
            return w_late[:, n - LAST, part] if LAST <= n < LAST + RING else split_view(n, part)

        def out_splits(c, i):
            n = TOTAL + c * OQ + i + LEAD
            if n < LAST:
                return [n]
            return {LAST: [LAST, LAST + 1, LAST + 2], LAST + 1: [LAST + 3, LAST + 4],
                    LAST + 2: [LAST + 5, LAST + 6], LAST + 3: [LAST + 7]}.get(n, [])

        def load_res(eng, c):
            eng.dma_start(x_res[:], x[0, :, c * NC:(c + 1) * NC].rearrange("(s p) d -> p s d", p=P)
                          ).then_inc(res_loaded, 16)

        block = ctx.enter_context(nc.Block())

        @block.sync
        def _(sp):
            def load_x(i):
                sp.dma_start(x_rows[:, :, i * 512:(i + 1) * 512],
                             x[0, :, i * 512:(i + 1) * 512].rearrange("(s p) d -> p s d", p=P)
                             ).then_inc(x_loaded[i], 16)

            def load_in(p, j):
                if not (isinstance(p, int) and p == 0 and j < RING):
                    sp.wait_ge(w_ready, p * QUARTERS + (j - RING + 1))
                kind, part = j // 4, j % 4
                rows = w_in[part * QK * P:(part + 1) * QK * P, bass.ds(p * PW + kind * D, PW)]
                sp.dma_start(w_raw[:, ring(j)].rearrange("p (k n) -> p k n", k=QK),
                             rows.rearrange("(k p) n -> p k n", p=P)).then_inc(raw_loaded[ring(j)], 16)

            def load_out(c, i):
                n = TOTAL + c * OQ + i
                sp.wait_ge(w_ready, n - RING + 1)
                rows = w_out[i * OK * P:(i + 1) * OK * P, c * NC:(c + 1) * NC]
                sp.dma_start(w_raw[:, ring(n)].rearrange("p (k n) -> p k n", k=OK),
                             rows.rearrange("(k p) n -> p k n", p=P)).then_inc(raw_loaded[ring(n)], 16)

            for i in range(4):
                load_x(i)
                load_in(0, i)
            for j in range(4, QUARTERS):
                load_in(0, j)
            with sp.Fori(1, PAIRS) as p:
                for j in range(QUARTERS):
                    load_in(p, j)
            for c in range(CHUNKS):
                if c == 0:
                    load_res(sp, 0)
                for i in range(OQ):
                    load_out(c, i)
                if c == 0:
                    sp.wait_ge(g_ready, PAIRS * ST)
                    sp.dma_start(ln_g_all, ln_g.unsqueeze(0).to_broadcast([P, D])).then_inc(ln_loaded, 16)
                    sp.dma_start(ln_b_all, ln_b.unsqueeze(0).to_broadcast([P, D])).then_inc(ln_loaded, 16)
            for s in range(ST):
                for half in range(2):
                    sp.wait_ge(rows_ready, 2 * s + half + 1)
                    cols = slice(half * D // 2, (half + 1) * D // 2)
                    sp.dma_start(out[0, s * P:(s + 1) * P, cols], r_rows[:, s, cols]).then_inc(out_stored, 16)
            sp.wait_ge(out_stored, 16 * 2 * ST)

        @block.gpsimd
        def _(pool):
            nc.gpsimd.memset(ident[:], 0.0).then_inc(ident_zero, 1)
            pool.wait_ge(ident_zero, 1)
            nc.gpsimd.affine_select(out=ident[:], in_=ident[:], compare_op=ALU.not_equal, fill=1.0, base=0,
                                    pattern=[[-1, P]], channel_multiplier=1).then_inc(consts_ready, 1)
            nc.gpsimd.memset(ones[:], 1.0).then_inc(consts_ready, 1)
            nc.gpsimd.memset(minus_half[:], -0.5).then_inc(consts_ready, 1)
            pool.wait_ge(bias_line_ready, 1)
            pool.dma_start(bias_dram.ap(), bias_line.unsqueeze(1).to_broadcast([16, P, BIAS_W])).then_inc(bias_stored, 16)
            pool.wait_ge(bias_stored, 16)
            for p in range(PAIRS):
                if p:
                    pool.wait_ge(max_ready, 2 * ST * p)
                pool.dma_start(bias[:], bass.AP(bias_dram, 2 * p * P * BIAS_W + P - 1,
                                                [[BIAS_W - 1, P], [P * BIAS_W, 2], [1, SEQ]])).then_inc(bias_loaded, 16)
                for t in range(ST):
                    n = ST * p + t + 1
                    pool.wait_ge(sq_ready, n)
                    nc.gpsimd.tensor_scalar(mean_sq[:, t:t + 1], sq_sum[:, t:t + 1], 1.0 / PW, EPS,
                                            ALU.mult, ALU.add).then_inc(mean_ready, 1)
                    pool.wait_ge(mean_ready, n)
                    nc.gpsimd.tensor_tensor(rms[:, t:t + 1], mean_sq[:, t:t + 1], minus_half[:],
                                            ALU.pow).then_inc(rms_ready, 1)
            for s in range(ST):
                pool.wait_ge(mv_ready, s + 1)
                nc.gpsimd.tensor_scalar(var_eps[:, s:s + 1], mean_var[:, s, 1:2], 1.0, EPS,
                                        ALU.mult, ALU.add).then_inc(var_ready, 1)
                pool.wait_ge(var_ready, s + 1)
                nc.gpsimd.tensor_tensor(r_std[:, s:s + 1], var_eps[:, s:s + 1], minus_half[:],
                                        ALU.pow).then_inc(r_std_ready, 1)

        @block.scalar
        def _(act):
            for i, vec in enumerate((lam_q1, lam_k1, lam_q2, lam_k2)):
                act.dma_start(lam_vecs[:, i:i + 1], vec.unsqueeze(1)).then_inc(small_loaded, 16)
            act.dma_start(table[0:BUCKETS, :], rel_bias).then_inc(table_loaded, 16)
            act.dma_start(onehot, bucket_onehot).then_inc(table_loaded, 16)
            for e in range(2):
                act.dma_start(sub_raw[:, e:e + 1], subln_g[e * P:(e + 1) * P].unsqueeze(1)).then_inc(sub_loaded, 16)

            def split_hi_at(p, j):
                a = j + LEAD
                act.wait_ge(raw_loaded[ring(a)], p * (16 * QUARTERS // RING) + 16 * (a // RING + 1))
                if not (isinstance(p, int) and p == 0 and j == 0):
                    act.wait_ge(quarter_done, p * QUARTERS + j)
                nc.scalar.activation(split_view(a, 0), w_raw[:, ring(a)], ACT.Copy).then_inc(w_hi, 1)

            def xT_split(i):
                act.wait_ge(xT_done, i + 1)
                nc.scalar.activation(xg_split[:, 0, i * 4:(i + 1) * 4], att[:], ACT.Copy).then_inc(xT_hi, 1)

            def chunk(p, c):
                act.wait_ge(quarter_done, p * QUARTERS + 4 * (c + 1))
                src = proj[:, 2 * (c % 2):2 * (c % 2) + 2]
                if c == 0:
                    nc.scalar.activation(qT[:, 0], src, ACT.Copy, scale=SCALE).then_inc(chunk_hi, 1)
                elif c == 1:
                    nc.scalar.activation(kT[:, 0], src, ACT.Copy).then_inc(chunk_hi, 1)
                elif c == 2:
                    nc.scalar.activation(v[:, 0], src.rearrange("p b (t e) -> p (b t) e", t=2),
                                         ACT.Copy).then_inc(chunk_hi, 1)
                else:
                    nc.scalar.activation(silu_z, src, ACT.Exp, scale=-1.0).then_inc(chunk_hi, 1)

            def exps(p, t):
                act.wait_ge(neg_max_ready, p * ST + t + 1)
                for h in range(2):
                    e = logits[:, h, 0:(t + 1) * P]
                    nc.scalar.activation(e, e, ACT.Exp, bias=neg_max[:, h:h + 1],
                                         accum_out=row_sum[:, h:h + 1]).then_inc(exp_ready, 1)

            def aT_split(p, t):
                if not (isinstance(p, int) and p == 0 and t < 2):
                    act.wait_ge(av_done, p * ST + t - 1)
                act.wait_ge(aT_done, p * ST + t + 1)
                nc.scalar.activation(aT[:, t % 2, 0, 0:(t + 1) * P], turned[:, 0:(t + 1) * P],
                                     ACT.Copy).then_inc(aT_hi, 1)

            def norm(p, t):
                if t == 0 and not (isinstance(p, int) and p == 0):
                    act.wait_ge(g_ready, p * ST)
                act.wait_ge(av_done, p * ST + t + 1)
                nc.scalar.activation(normed[:, t], av, ACT.Square, scale=inv_sum[:, t, 0:1],
                                     accum_out=sq_sum[:, t:t + 1]).then_inc(sq_ready, 1)
                act.wait_ge(o_scale_ready, p * ST + t + 1)
                nc.scalar.activation(normed[:, t], av, ACT.Copy,
                                     scale=o_scale[:, t:t + 1]).then_inc(normed_ready, 1)

            def late_steps(p, j):
                if j == 0:
                    chunk(p, 3)
                if j <= 1:
                    norm(p, j + 2)

            def own_steps(p, j):
                if j in (4, 8, 12):
                    chunk(p, j // 4 - 1)
                if 10 <= j < 14:
                    exps(p, j - 10)
                if j >= 12:
                    aT_split(p, j - 12)
                if j >= 14:
                    norm(p, j - 14)

            for i in range(4):
                xT_split(i)
                if i < LEAD:
                    act.wait_ge(raw_loaded[i], 16)
                    nc.scalar.activation(split_view(i, 0), w_raw[:, i], ACT.Copy).then_inc(w_hi, 1)
                if i == 0:
                    act.wait_ge(lam_sums, 1)
                    nc.scalar.activation(lam_exp[:], proj[:, 3, 0:2], ACT.Exp).then_inc(lam_exped, 1)
            for j in range(QUARTERS):
                split_hi_at(0, j)
                own_steps(0, j)
            with act.Fori(1, PAIRS) as p:
                for j in range(QUARTERS):
                    split_hi_at(p, j)
                    late_steps(p - 1, j)
                    own_steps(p, j)

            def g_split_hi(i):
                if i == OQ - 1:
                    act.wait_ge(g_ready, PAIRS * ST)
                else:
                    act.wait_ge(g_ready, (PAIRS - 1) * ST)
                act.wait_ge(quarter_done, TOTAL)
                nc.scalar.activation(xg_split[:, 0, 2 * i:2 * i + 2], g[:, 2 * i:2 * i + 2],
                                     ACT.Copy).then_inc(g_hi, 1)

            for c in range(CHUNKS):
                for i in range(OQ):
                    if c == 0 and i < OQ - 1:
                        g_split_hi(i)
                    for n in out_splits(c, i):
                        act.wait_ge(raw_loaded[ring(n)], 16 * (n // RING + 1))
                        if n < LAST:
                            act.wait_ge(quarter_done, n - LEAD)
                        elif n >= LAST + RING:
                            act.wait_ge(quarter_done, n - LEAD - RING)
                        nc.scalar.activation(out_split_view(n, 0), w_raw[:, ring(n)], ACT.Copy).then_inc(w_hi, 1)
                    if c == 0:
                        late_steps(PAIRS - 1, i)
                        if i == OQ - 2:
                            g_split_hi(OQ - 1)
                    elif i == ST:
                        act.wait_ge(r_ready, ST * c)
                        load_res(act, c)

        @block.vector
        def _(dve):
            nc.vector.memset(table[BUCKETS:BUCKETS + 1, :], MASKED).then_inc(mask_ready, 1)
            dve.wait_ge(small_loaded, 64)
            lv = lam_vecs[:].rearrange("p (i j) -> p i j", j=2)
            nc.vector.tensor_tensor(lam_prod[:], lv[:, :, 0], lv[:, :, 1], ALU.mult).then_inc(lam_step, 1)
            dve.wait_ge(sub_loaded, 32)
            nc.vector.tensor_scalar(sub_g[:], sub_raw[:], 1.0 - LAM_INIT, None, ALU.mult).then_inc(lam_step, 1)

            def split_lo_at(p, j):
                a = j + LEAD
                dve.wait_ge(w_hi, p * QUARTERS + a + 1)
                nc.vector.tensor_tensor(split_view(a, 1), w_raw[:, ring(a)],
                                        split_view(a, 0).bitcast(F32), ALU.subtract).then_inc(w_ready, 1)

            def xT_split(i):
                dve.wait_ge(xT_hi, i + 1)
                tiles = slice(i * 4, (i + 1) * 4)
                nc.vector.tensor_tensor(xg_split[:, 1, tiles], att[:], xg_split[:, 0, tiles].bitcast(F32),
                                        ALU.subtract).then_inc(xT_ready, 1)

            def chunk(p, c):
                dve.wait_ge(chunk_hi, p * 4 + c + 1)
                src = proj[:, 2 * (c % 2):2 * (c % 2) + 2]
                if c == 0:
                    nc.vector.scalar_tensor_tensor(qT[:, 1], src, SCALE, qT[:, 0].bitcast(F32),
                                                   ALU.mult, ALU.subtract).then_inc(chunk_moved, 1)
                elif c == 1:
                    nc.vector.tensor_tensor(kT[:, 1], src, kT[:, 0].bitcast(F32),
                                            ALU.subtract).then_inc(chunk_moved, 1)
                elif c == 2:
                    nc.vector.tensor_tensor(v[:, 1], src.rearrange("p b (t e) -> p (b t) e", t=2),
                                            v[:, 0].bitcast(F32), ALU.subtract).then_inc(chunk_moved, 1)
                else:
                    nc.vector.tensor_scalar(silu_z, silu_z, 1.0, None, ALU.add).then_inc(z_step, 1)
                    dve.wait_ge(z_step, p * 2 + 1)
                    nc.vector.reciprocal(silu_z, silu_z).then_inc(z_step, 1)
                    dve.wait_ge(z_step, p * 2 + 2)
                    for e in range(2):
                        last = nc.vector.scalar_tensor_tensor(silu_z[:, e], src[:, e], sub_g[:, e:e + 1],
                                                              silu_z[:, e], ALU.mult, ALU.mult)
                    last.then_inc(chunk_moved, 1)

            def logits_of(p, t):
                dve.wait_ge(scores_done, p * ST + t + 1)
                if not (isinstance(p, int) and p == 0 and t == 0):
                    dve.wait_ge(a_ready, p * ST + t)
                if t == 0:
                    dve.wait_ge(bias_loaded, p * 16 + 16)
                dve.sem_inc(tile_begun, 1)
                for h in range(2):
                    nc.vector.tensor_tensor_reduce(
                        out=logits[:, h, 0:(t + 1) * P], in0=scores[:, h, 0:(t + 1) * P],
                        in1=bias[:, h, (ST - 1 - t) * P:SEQ], scale=1.0, scalar=LOWEST,
                        op0=ALU.add, op1=ALU.max, accum_out=row_max[:, h:h + 1]).then_inc(max_ready, 1)
                dve.wait_ge(max_ready, (p * ST + t + 1) * 2)
                nc.vector.tensor_scalar(neg_max[:], row_max[:], -1.0, None, ALU.mult).then_inc(neg_max_ready, 1)

            def combine(p, t):
                n = p * ST + t + 1
                if not (isinstance(p, int) and p == 0):
                    dve.wait_ge(normed_ready, n - ST)
                dve.wait_ge(exp_ready, n * 2)
                nc.vector.reciprocal(inv_sum[:, t], row_sum[:]).then_inc(inv_ready, 1)
                dve.wait_ge(inv_ready, n)
                nc.vector.scalar_tensor_tensor(mix[:], row_sum[:, 0:1], neg_lam[:], inv_sum[:, t, 1:2],
                                               ALU.mult, ALU.mult).then_inc(mix_ready, 1)
                if not (isinstance(p, int) and p == 0 and t < 2):
                    dve.wait_ge(aT_done, n - 2)
                dve.wait_ge(mix_ready, n)
                cols = slice(0, (t + 1) * P)
                nc.vector.scalar_tensor_tensor(a_rows[:, t % 2, cols], logits[:, 1, cols], mix[:],
                                               logits[:, 0, cols], ALU.mult, ALU.add).then_inc(a_ready, 1)

            def aT_split(p, t):
                dve.wait_ge(aT_hi, p * ST + t + 1)
                cols = slice(0, (t + 1) * P)
                nc.vector.tensor_tensor(aT[:, t % 2, 1, cols], turned[:, cols],
                                        aT[:, t % 2, 0, cols].bitcast(F32), ALU.subtract).then_inc(aT_ready, 1)

            def norm(p, t):
                dve.wait_ge(rms_ready, p * ST + t + 1)
                nc.vector.tensor_tensor(o_scale[:, t:t + 1], rms[:, t:t + 1], inv_sum[:, t, 0:1],
                                        ALU.mult).then_inc(o_scale_ready, 1)

            def gate(p, t):
                dve.wait_ge(nT_done, p * ST + t + 1)
                if t == 0:
                    dve.wait_ge(chunk_moved, p * 4 + 4)
                turned_n = turned[:, 0:PW].rearrange("p (e s) -> p e s", e=2)
                rows = slice(t * P, (t + 1) * P)
                nc.vector.tensor_tensor(g[:, bass.ds(p * 2, 2), rows], turned_n, silu_z[:, :, rows],
                                        ALU.mult).then_inc(g_ready, 1)

            def late_steps(p, j):
                if j == 0:
                    chunk(p, 3)
                if j <= 1:
                    norm(p, j + 2)
                if 1 <= j <= 4:
                    gate(p, j - 1)

            def slot(p, j, late):
                if 10 <= j < 14:
                    logits_of(p, j - 10)
                split_lo_at(p, j)
                if late:
                    late_steps(p - 1, j)
                if 10 <= j < 14:
                    combine(p, j - 10)
                if j in (4, 8, 12):
                    chunk(p, j // 4 - 1)
                if j >= 12:
                    aT_split(p, j - 12)
                if j >= 14:
                    norm(p, j - 14)

            for i in range(4):
                xT_split(i)
                if i < LEAD:
                    dve.wait_ge(w_hi, i + 1)
                    nc.vector.tensor_tensor(split_view(i, 1), w_raw[:, i], split_view(i, 0).bitcast(F32),
                                            ALU.subtract).then_inc(w_ready, 1)
                if i == 0:
                    dve.wait_ge(lam_exped, 1)
                    nc.vector.tensor_tensor(lam_diff[:], lam_exp[:, 1:2], lam_exp[:, 0:1],
                                            ALU.subtract).then_inc(lam_step, 1)
                    dve.wait_ge(lam_step, 3)
                    nc.vector.tensor_scalar(neg_lam[:], lam_diff[:], LAM_INIT, None,
                                            ALU.subtract).then_inc(lam_step, 1)
                    dve.wait_ge(lam_step, 4)
                    dve.wait_ge(bias_line_done, 1)
                    nc.vector.tensor_copy(bias_line.rearrange("h (a b) -> h a b", a=2),
                                          proj[0:16, 1:3, 0:BIAS_W // 2]).then_inc(bias_line_ready, 1)
            for j in range(QUARTERS):
                slot(0, j, False)
            with dve.Fori(1, PAIRS) as p:
                for j in range(QUARTERS):
                    slot(p, j, True)

            def g_split_lo(i):
                dve.wait_ge(g_hi, i + 1)
                tiles = slice(2 * i, 2 * i + 2)
                nc.vector.tensor_tensor(xg_split[:, 1, tiles], g[:, tiles], xg_split[:, 0, tiles].bitcast(F32),
                                        ALU.subtract).then_inc(g_split, 1)

            def out_banks(c):
                return proj if c % 2 == 0 else att

            def residual(c, s):
                dve.wait_ge(res_loaded, 16 * (c + 1))
                nc.vector.scalar_tensor_tensor(r_rows[:, s, c * NC:(c + 1) * NC], x_res[:, s], ALPHA,
                                               out_banks(c)[:, s], ALU.mult, ALU.add).then_inc(r_ready, 1)
                dve.wait_ge(r_ready, ST * c + s + 1)
                nc.vector.bn_stats(stats[:, s, c], r_rows[:, s, c * NC:(c + 1) * NC]).then_inc(stats_ready, 1)

            for c in range(CHUNKS):
                for i in range(OQ):
                    if c == 0 and i < OQ - 1:
                        g_split_lo(i)
                    for n in out_splits(c, i):
                        dve.wait_ge(w_hi, n + 1)
                        nc.vector.tensor_tensor(out_split_view(n, 1), w_raw[:, ring(n)],
                                                out_split_view(n, 0).bitcast(F32),
                                                ALU.subtract).then_inc(w_ready, 1)
                    if c == 0:
                        late_steps(PAIRS - 1, i)
                        if i == OQ - 2:
                            g_split_lo(OQ - 1)
                    elif i < ST:
                        if i == 0:
                            dve.wait_ge(quarter_done, TOTAL + OQ * c)
                        residual(c - 1, i)
            for s in range(ST):
                c = CHUNKS - 1
                dve.wait_ge(tile_done, s + 1)
                residual(c, s)
                dve.wait_ge(stats_ready, ST * c + s + 1)
                nc.vector.bn_aggr(mean_var[:, s], stats[:, s].rearrange("p c k -> p (c k)")).then_inc(mv_ready, 1)
                dve.wait_ge(mv_ready, s + 1)
                if s == 0:
                    dve.wait_ge(ln_loaded, 32)
                halves = [slice(h * D // 2, (h + 1) * D // 2) for h in range(2)]
                for h, cols in enumerate(halves):
                    nc.vector.scalar_tensor_tensor(r_rows[:, s, cols], r_rows[:, s, cols], mean_var[:, s, 0:1],
                                                   ln_g_all[:, cols], ALU.subtract, ALU.mult).then_inc(centred, 1)
                dve.wait_ge(r_std_ready, s + 1)
                for h, cols in enumerate(halves):
                    dve.wait_ge(centred, 2 * s + h + 1)
                    nc.vector.scalar_tensor_tensor(r_rows[:, s, cols], r_rows[:, s, cols], r_std[:, s:s + 1],
                                                   ln_b_all[:, cols], ALU.mult, ALU.add).then_inc(rows_ready, 1)

        @block.tensor
        def _(pe):
            def mm(dst, lhsT, rhs, start, stop):
                return nc.tensor.matmul(dst, lhsT, rhs, start=start, stop=stop, skip_group_check=True)

            pe.wait_ge(table_loaded, 32)
            pe.wait_ge(mask_ready, 1)
            pe.wait_ge(consts_ready, 3)
            for i in range(2):
                last = nc.tensor.matmul(proj[0:16, 1 + i, 0:BIAS_W // 2], table[:],
                                        onehot[:, i * BIAS_W // 2:(i + 1) * BIAS_W // 2], start=True, stop=True)
            last.then_inc(bias_line_done, 1)
            pe.wait_ge(lam_step, 1)
            nc.tensor.matmul(proj[:, 3, 0:2], ones[:], lam_prod[:], start=True, stop=True).then_inc(lam_sums, 1)

            def turn_x(i):
                pe.wait_ge(x_loaded[i], 16)
                if i:
                    pe.wait_ge(xT_ready, i)
                for k in range(4):
                    for s in range(ST):
                        col = (4 * i + k) * P
                        last = nc.tensor.transpose(att[:, k, s * P:(s + 1) * P], x_rows[:, s, col:col + P],
                                                   ident[:])
                last.then_inc(xT_done, 1)

            def quarter(p, j):
                c, part = j // 4, j % 4
                pe.wait_ge(w_ready, p * QUARTERS + j + 1)
                if part == 0 and not (isinstance(p, int) and p == 0 and c < 2):
                    pe.wait_ge(chunk_moved, p * 4 + (c - 1))
                w = [split_view(j, l).rearrange("p (k n) -> p k n", k=QK) for l in range(2)]
                bank = 2 * (c % 2)
                for kk in range(QK):
                    k = part * QK + kk
                    x_hi, x_lo = xg_split[:, 0, k], xg_split[:, 1, k]
                    first, final = k == 0, k == KT - 1
                    if c == 2:
                        for s in range(ST):
                            rows = slice(s * P, (s + 1) * P)
                            dst = proj[:, bank + s // 2, (s % 2) * PW:(s % 2 + 1) * PW]
                            mm(dst, x_hi[:, rows], w[0][:, kk], first and s % 2 == 0, False)
                            mm(dst, x_hi[:, rows], w[1][:, kk], False, False)
                            last = mm(dst, x_lo[:, rows], w[0][:, kk], False, final and s % 2 == 1)
                    else:
                        for e in range(2):
                            cols = slice(e * P, (e + 1) * P)
                            dst = proj[:, bank + e]
                            mm(dst, w[0][:, kk, cols], x_hi, first, False)
                            mm(dst, w[0][:, kk, cols], x_lo, False, False)
                            last = mm(dst, w[1][:, kk, cols], x_hi, False, final)
                last.then_inc(quarter_done, 1)

            def scores_of(p, t):
                if t == 0:
                    pe.wait_ge(chunk_moved, p * 4 + 2)
                if t:
                    pe.wait_ge(max_ready, p * (2 * ST) + 2 * t)
                n = max(t + 1, 2) * P
                rows = slice(t * P, (t + 1) * P)
                for h in range(2):
                    dst = scores[:, h, 0:n]
                    mm(dst, qT[:, 0, h, rows], kT[:, 0, h, 0:n], True, False)
                    mm(dst, qT[:, 0, h, rows], kT[:, 1, h, 0:n], False, False)
                    last = mm(dst, qT[:, 1, h, rows], kT[:, 0, h, 0:n], False, True)
                last.then_inc(scores_done, 1)

            def turn_a(p, t):
                pe.wait_ge(a_ready, p * ST + t + 1)
                if t == 0:
                    if not (isinstance(p, int) and p == 0):
                        pe.wait_ge(g_ready, p * ST)
                else:
                    pe.wait_ge(aT_ready, p * ST + t)
                for kt in range(t + 1):
                    cols = slice(kt * P, (kt + 1) * P)
                    last = nc.tensor.transpose(turned[:, cols], a_rows[:, t % 2, cols], ident[:])
                last.then_inc(aT_done, 1)

            def weigh_v(p, t):
                pe.wait_ge(aT_ready, p * ST + t + 1)
                if t == 0:
                    pe.wait_ge(chunk_moved, p * 4 + 3)
                if not (isinstance(p, int) and p == 0 and t == 0):
                    pe.wait_ge(normed_ready, p * ST + t)
                dst = av
                for kt in range(t + 1):
                    cols = slice(kt * P, (kt + 1) * P)
                    a_hi, a_lo = aT[:, t % 2, 0, cols], aT[:, t % 2, 1, cols]
                    mm(dst, a_hi, v[:, 0, kt], kt == 0, False)
                    mm(dst, a_hi, v[:, 1, kt], False, False)
                    last = mm(dst, a_lo, v[:, 0, kt], False, kt == t)
                last.then_inc(av_done, 1)

            def turn_normed(p, t):
                pe.wait_ge(normed_ready, p * ST + t + 1)
                if t == 0:
                    pe.wait_ge(aT_ready, p * ST + ST)
                else:
                    pe.wait_ge(g_ready, p * ST + t)
                for e in range(2):
                    last = nc.tensor.transpose(turned[:, e * P:(e + 1) * P],
                                               normed[:, t, e * P:(e + 1) * P], ident[:])
                last.then_inc(nT_done, 1)

            def late_inserts(p, j):
                if j == 0:
                    weigh_v(p, 3)
                if j < 4:
                    turn_normed(p, j)

            def own_inserts(p, j):
                if 9 <= j < 13:
                    scores_of(p, j - 9)
                if 11 <= j < 15:
                    turn_a(p, j - 11)
                if 13 <= j:
                    weigh_v(p, j - 13)

            turn_x(0)
            pe.wait_ge(lam_exped, 1)
            pe.wait_ge(bias_line_ready, 1)
            for j in range(QUARTERS):
                if j < 4:
                    pe.wait_ge(xT_ready, j + 1)
                quarter(0, j)
                if j < 3:
                    turn_x(j + 1)
                own_inserts(0, j)
            with pe.Fori(1, PAIRS) as p:
                for j in range(QUARTERS):
                    quarter(p, j)
                    late_inserts(p - 1, j)
                    own_inserts(p, j)

            def out_product(c, i, s, w_hi_part, w_lo_part, first, final):
                dst = (proj if c % 2 == 0 else att)[:, s]
                for kk in range(OK):
                    k = i * OK + kk
                    rows = slice(s * P, (s + 1) * P)
                    g_hi_part, g_lo_part = xg_split[:, 0, k, rows], xg_split[:, 1, k, rows]
                    wh = w_hi_part.rearrange("p (k n) -> p k n", k=OK)[:, kk]
                    wl = w_lo_part.rearrange("p (k n) -> p k n", k=OK)[:, kk]
                    mm(dst, g_hi_part, wh, first and kk == 0, False)
                    mm(dst, g_hi_part, wl, False, False)
                    last = mm(dst, g_lo_part, wh, False, final and kk == OK - 1)
                return last

            for c in range(CHUNKS - 1):
                for i in range(OQ):
                    n = TOTAL + c * OQ + i
                    pe.wait_ge(w_ready, n + 1)
                    if c == 0:
                        pe.wait_ge(g_split, i + 1)
                        if i == 0:
                            pe.wait_ge(chunk_moved, 4 * PAIRS)
                    elif i == 0 and c == 2:
                        pe.wait_ge(r_ready, ST)
                    for s in range(ST):
                        last = out_product(c, i, s, split_view(n, 0), split_view(n, 1), i == 0, i == OQ - 1)
                    last.then_inc(quarter_done, 1)
                    if c == 0:
                        late_inserts(PAIRS - 1, i)
            pe.wait_ge(r_ready, 2 * ST)
            for s in range(ST):
                for i in range(OQ):
                    n = LAST + i
                    if s == 0:
                        pe.wait_ge(w_ready, n + 1)
                    last = out_product(CHUNKS - 1, i, s, out_split_view(n, 0), out_split_view(n, 1),
                                       i == 0, i == OQ - 1)
                last.then_inc(tile_done, 1)


LAST = PAIRS * QUARTERS + (CHUNKS - 1) * OQ

_INS = ["x", "rel_bias", "w_in_0", "lam_q1_0", "lam_k1_0", "lam_q2_0", "lam_k2_0", "subln_g_0", "w_out_0",
        "ln_g_0", "ln_b_0"]


def _bucket_onehot():
    import numpy as np
    dist = SEQ - 1 - np.arange(BIAS_W)
    n = np.maximum(dist, 1).astype(np.float32)
    exact = BUCKETS // 2
    large = exact + (np.log(n / np.float32(exact)) / np.float32(math.log(128 / exact))
                     * np.float32(BUCKETS - exact)).astype(np.int32)
    bucket = np.where(dist < exact, dist, np.minimum(large, BUCKETS - 1))
    bucket = np.where(dist < 0, BUCKETS, bucket)
    return (np.arange(BUCKETS + 1)[:, None] == bucket[None, :]).astype(np.float32)


def kernel(**inputs):
    import numpy as _np
    import concourse.bacc as _bacc
    from concourse import mybir as _mybir
    from concourse.bass_utils import run_bass_kernel_spmd as _run

    nc = _bacc.Bacc("TRN2", target_bir_lowering=False, num_devices=1)
    arrays, args = {}, []
    for name in _INS:
        a = _np.ascontiguousarray(inputs[name])
        arrays[f"in_{name}_dram"] = a
        args.append(nc.dram_tensor(f"in_{name}_dram", a.shape, _mybir.dt.from_np(a.dtype), kind="ExternalInput").ap())
    onehot = _bucket_onehot()
    arrays["bucket_onehot_dram"] = onehot
    args.append(nc.dram_tensor("bucket_onehot_dram", onehot.shape, _mybir.dt.from_np(onehot.dtype),
                               kind="ExternalInput").ap())
    args.append(nc.dram_tensor("out_dram", (1, SEQ, D), _mybir.dt.float32, kind="ExternalOutput").ap())
    diff_layer(nc, *args)
    r = _run(nc, [arrays], core_ids=[0])
    return r.results[0]["out_dram"]
```

```python
from contextlib import ExitStack
import math

import concourse.bass as bass
from concourse import mybir

ALU = mybir.AluOpType
ACT = mybir.ActivationFunctionType
F32 = mybir.dt.float32
F32R = mybir.dt.float32r

P = 128
SEQ = 512
D = 2048
PAIRS = 8
PW = D // PAIRS
HD = PW // 2
ST = SEQ // P
XK = 2
KT = D // P
XU = KT // XK
QK = 4
QUARTERS = 4 * 4
QE = QK * PW
EARLY = 4
RING = 4
LEAD = RING - 1
NC = 512
CHUNKS = D // NC
OK = QE // NC
OQ = KT // OK
BUCKETS = 32
BIAS_W = 640
SCALE = float(HD) ** -0.5
LAM_INIT = 0.8 - 0.6 * math.exp(-0.3 * 0)
ALPHA = 2.0 ** 0.25
EPS = 1e-5
MASKED = -1e30
LOWEST = -3.0e38


def diff_layer(nc, x, rel_bias, w_in, lam_q1, lam_k1, lam_q2, lam_k2, subln_g, w_out, ln_g, ln_b,
               bucket_onehot, out):
    with ExitStack() as ctx:
        def sb(name, shape, dt=F32):
            return ctx.enter_context(nc.sbuf_tensor(name, shape, dt))

        def sem(name):
            return ctx.enter_context(nc.semaphore(name))

        xg_split = sb("xg_split", [P, 2, KT, SEQ], F32R)
        big = sb("big", [P, D * ST])
        x_rows = big[:].rearrange("p (s d) -> p s d", s=ST)
        g = big[:].rearrange("p (k s) -> p k s", k=KT)
        r_rows = x_rows
        w_raw = sb("w_raw", [P, RING, QE])
        w_split = sb("w_split", [P, RING, 2, QE], F32R)
        operands = sb("operands", [P, 8 * QE], F32R)
        qT = operands[:, 0:2 * QE].rearrange("p (l h s) -> p l h s", l=2, h=2)
        kT = operands[:, 2 * QE:4 * QE].rearrange("p (l h s) -> p l h s", l=2, h=2)
        v = operands[:, 4 * QE:6 * QE].rearrange("p (l t e) -> p l t e", l=2, t=ST)
        aT = operands[:, 6 * QE:8 * QE].rearrange("p (b l s) -> p b l s", b=2, l=2)
        w_late = operands[:].rearrange("p (q l e) -> p q l e", q=4, l=2)
        g_early = operands[:, 0:4 * QE].rearrange("p (l k s) -> p l k s", l=2, k=EARLY)
        scratch = sb("scratch", [P, 2 * D])
        logits = scratch[:, 0:1024].rearrange("p (h s) -> p h s", h=2)
        a_rows = scratch[:, 1024:2048].rearrange("p (b s) -> p b s", b=2)
        silu_z = scratch[:, 2048:3072].rearrange("p (e s) -> p e s", e=2)
        normed = scratch[:, 3072:4096].rearrange("p (t e) -> p t e", t=ST)
        onehot = scratch[0:BUCKETS + 1, 0:BIAS_W]
        bias_line = scratch[0:16, 1024:1024 + BIAS_W]
        ln_g_all, ln_b_all = scratch[:, 0:D], scratch[:, D:2 * D]
        bias = sb("bias", [P, 2, SEQ])
        x_res = sb("x_res", [P, ST, NC])
        z_gain = x_res[:, 0:2]
        ident = sb("ident", [P, P])
        ones = sb("ones", [P, P])
        table = sb("table", [BUCKETS + 1, 16])
        lam_vecs = sb("lam_vecs", [P, 4])
        lam_prod = sb("lam_prod", [P, 2])
        lam_exp = sb("lam_exp", [P, 2])
        lam_diff = sb("lam_diff", [P, 1])
        neg_lam = sb("neg_lam", [P, 1])
        sub_raw = sb("sub_raw", [P, 2])
        sub_g = sb("sub_g", [P, 2])
        minus_half = sb("minus_half", [P, 1])
        row_max = sb("row_max", [P, 2])
        neg_max = sb("neg_max", [P, 2])
        row_sum = sb("row_sum", [P, 2])
        inv_sum = sb("inv_sum", [P, ST, 2])
        mix = sb("mix", [P, 1])
        sq_sum = sb("sq_sum", [P, ST])
        mean_sq = sb("mean_sq", [P, ST])
        rms = sb("rms", [P, ST])
        o_scale = sb("o_scale", [P, ST])
        stats = sb("stats", [P, ST, CHUNKS, 6])
        mean_var = sb("mean_var", [P, ST, 2])
        var_eps = sb("var_eps", [P, ST])
        r_std = sb("r_std", [P, ST])
        shift = sb("shift", [P, ST])
        bias_dram = nc.dram_tensor("bias_by_distance", (16, P, BIAS_W), F32, kind="Internal")

        proj = ctx.enter_context(nc.psum_tensor("proj", [P, 4, 512], F32))
        att = ctx.enter_context(nc.psum_tensor("att", [P, 4, 512], F32))
        scores = att[:, 0:2]
        turned = att[:, 2]
        av = att[:, 3, 0:PW]

        def unit_banks(u):
            return (att[:, 0:2], att[:, 2:4], proj[:, 2:4])[u % 3]

        x_loaded = [sem(f"x_loaded{i}") for i in range(XU)]
        raw_loaded = [sem(f"raw_loaded{i}") for i in range(RING)]
        small_loaded = sem("small_loaded")
        sub_loaded = sem("sub_loaded")
        table_loaded = sem("table_loaded")
        bias_stored = sem("bias_stored")
        bias_loaded = sem("bias_loaded")
        res_loaded = sem("res_loaded")
        ln_loaded = sem("ln_loaded")
        out_stored = sem("out_stored")
        ident_zero = sem("ident_zero")
        consts_ready = sem("consts_ready")
        mask_ready = sem("mask_ready")
        bias_line_done = sem("bias_line_done")
        bias_line_ready = sem("bias_line_ready")
        lam_step = sem("lam_step")
        sub_ready = sem("sub_ready")
        lam_sums = sem("lam_sums")
        lam_exped = sem("lam_exped")
        xT_done = sem("xT_done")
        xT_hi = sem("xT_hi")
        xT_ready = sem("xT_ready")
        w_hi = sem("w_hi")
        w_ready = sem("w_ready")
        quarter_done = sem("quarter_done")
        chunk_hi = sem("chunk_hi")
        chunk_moved = sem("chunk_moved")
        z_moved = sem("z_moved")
        z_denom = sem("z_denom")
        z_inv = sem("z_inv")
        silu_ready = sem("silu_ready")
        scores_done = sem("scores_done")
        tile_begun = sem("tile_begun")
        max_ready = sem("max_ready")
        neg_max_ready = sem("neg_max_ready")
        exp_ready = sem("exp_ready")
        inv_ready = sem("inv_ready")
        mix_ready = sem("mix_ready")
        a_ready = sem("a_ready")
        aT_done = sem("aT_done")
        aT_hi = sem("aT_hi")
        aT_ready = sem("aT_ready")
        av_done = sem("av_done")
        sq_ready = sem("sq_ready")
        mean_ready = sem("mean_ready")
        rms_ready = sem("rms_ready")
        o_scale_ready = sem("o_scale_ready")
        normed_ready = sem("normed_ready")
        nT_done = sem("nT_done")
        g_ready = sem("g_ready")
        g_hi = sem("g_hi")
        g_split = sem("g_split")
        tile_done = sem("tile_done")
        r_ready = sem("r_ready")
        stats_ready = sem("stats_ready")
        mv_ready = sem("mv_ready")
        var_ready = sem("var_ready")
        r_std_ready = sem("r_std_ready")
        shift_ready = sem("shift_ready")
        act_normed = sem("act_normed")
        pool_scaled = sem("pool_scaled")
        pool_rows_ready = sem("pool_rows_ready")
        centred = sem("centred")
        rows_ready = sem("rows_ready")

        TOTAL = PAIRS * QUARTERS

        def ring(n):
            return n % RING

        def split_view(n_static, part):
            return w_split[:, ring(n_static), part]

        def out_split_view(n, part):
            return w_late[:, n - LAST, part] if LAST <= n < LAST + RING else split_view(n, part)

        def out_splits(c, i):
            n = TOTAL + c * OQ + i + LEAD
            if n < LAST:
                return [n]
            return {LAST: [LAST, LAST + 1, LAST + 2], LAST + 1: [LAST + 3, LAST + 4],
                    LAST + 2: [LAST + 5, LAST + 6], LAST + 3: [LAST + 7]}.get(n, [])

        def load_res(eng, c):
            eng.dma_start(x_res[:], x[0, :, c * NC:(c + 1) * NC].rearrange("(s p) d -> p s d", p=P)
                          ).then_inc(res_loaded, 16)

        block = ctx.enter_context(nc.Block())

        @block.sync
        def _(sp):
            def load_x(i):
                cols = slice(i * XK * P, (i + 1) * XK * P)
                sp.dma_start(x_rows[:, :, cols], x[0, :, cols].rearrange("(s p) d -> p s d", p=P)
                             ).then_inc(x_loaded[i], 16)

            def load_in(p, j):
                if not (isinstance(p, int) and p == 0 and j < RING):
                    sp.wait_ge(w_ready, p * QUARTERS + (j - RING + 1))
                kind, part = j // 4, j % 4
                rows = w_in[part * QK * P:(part + 1) * QK * P, bass.ds(p * PW + kind * D, PW)]
                sp.dma_start(w_raw[:, ring(j)].rearrange("p (k n) -> p k n", k=QK),
                             rows.rearrange("(k p) n -> p k n", p=P)).then_inc(raw_loaded[ring(j)], 16)

            def load_out(c, i):
                n = TOTAL + c * OQ + i
                sp.wait_ge(w_ready, n - RING + 1)
                rows = w_out[i * OK * P:(i + 1) * OK * P, c * NC:(c + 1) * NC]
                sp.dma_start(w_raw[:, ring(n)].rearrange("p (k n) -> p k n", k=OK),
                             rows.rearrange("(k p) n -> p k n", p=P)).then_inc(raw_loaded[ring(n)], 16)

            for i in range(4):
                load_x(2 * i)
                load_x(2 * i + 1)
                load_in(0, i)
            sp.dma_start(table[0:BUCKETS, :], rel_bias).then_inc(table_loaded, 16)
            sp.dma_start(onehot, bucket_onehot).then_inc(table_loaded, 16)
            for i, vec in enumerate((lam_q1, lam_k1, lam_q2, lam_k2)):
                sp.dma_start(lam_vecs[:, i:i + 1], vec.unsqueeze(1)).then_inc(small_loaded, 16)
            for e in range(2):
                sp.dma_start(sub_raw[:, e:e + 1], subln_g[e * P:(e + 1) * P].unsqueeze(1)).then_inc(sub_loaded, 16)
            for j in range(4, QUARTERS):
                load_in(0, j)
            with sp.Fori(1, PAIRS) as p:
                for j in range(QUARTERS):
                    load_in(p, j)
            for c in range(CHUNKS):
                for i in range(OQ):
                    load_out(c, i)
                if c == 1:
                    sp.wait_ge(g_ready, PAIRS * ST)
                    sp.dma_start(ln_g_all, ln_g.unsqueeze(0).to_broadcast([P, D])).then_inc(ln_loaded, 16)
                    sp.dma_start(ln_b_all, ln_b.unsqueeze(0).to_broadcast([P, D])).then_inc(ln_loaded, 16)
            for s in range(ST):
                for cols in VECTOR_PIECES:
                    sp.wait_ge(rows_ready, len(VECTOR_PIECES) * s + VECTOR_PIECES.index(cols) + 1)
                    sp.dma_start(out[0, s * P:(s + 1) * P, cols], r_rows[:, s, cols]).then_inc(out_stored, 16)
                sp.wait_ge(pool_rows_ready, s + 1)
                sp.dma_start(out[0, s * P:(s + 1) * P, POOL_PIECE], r_rows[:, s, POOL_PIECE]
                             ).then_inc(out_stored, 16)
            sp.wait_ge(out_stored, 16 * (len(VECTOR_PIECES) + 1) * ST)

        @block.gpsimd
        def _(pool):
            nc.gpsimd.memset(ident[:], 0.0).then_inc(ident_zero, 1)
            pool.wait_ge(ident_zero, 1)
            nc.gpsimd.affine_select(out=ident[:], in_=ident[:], compare_op=ALU.not_equal, fill=1.0, base=0,
                                    pattern=[[-1, P]], channel_multiplier=1).then_inc(consts_ready, 1)
            nc.gpsimd.memset(ones[:], 1.0).then_inc(consts_ready, 1)
            nc.gpsimd.memset(minus_half[:], -0.5).then_inc(consts_ready, 1)
            pool.wait_ge(bias_line_ready, 1)
            pool.dma_start(bias_dram.ap(), bias_line.unsqueeze(1).to_broadcast([16, P, BIAS_W])).then_inc(bias_stored, 16)
            pool.wait_ge(bias_stored, 16)
            for p in range(PAIRS):
                if p:
                    pool.wait_ge(max_ready, 2 * ST * p)
                pool.dma_start(bias[:], bass.AP(bias_dram, 2 * p * P * BIAS_W + P - 1,
                                                [[BIAS_W - 1, P], [P * BIAS_W, 2], [1, SEQ]])).then_inc(bias_loaded, 16)
                for t in range(ST):
                    n = ST * p + t + 1
                    pool.wait_ge(sq_ready, n)
                    nc.gpsimd.tensor_scalar(mean_sq[:, t:t + 1], sq_sum[:, t:t + 1], 1.0 / PW, EPS,
                                            ALU.mult, ALU.add).then_inc(mean_ready, 1)
                    pool.wait_ge(mean_ready, n)
                    nc.gpsimd.tensor_tensor(rms[:, t:t + 1], mean_sq[:, t:t + 1], minus_half[:],
                                            ALU.pow).then_inc(rms_ready, 1)
            for s in range(ST):
                pool.wait_ge(mv_ready, s + 1)
                nc.gpsimd.tensor_scalar(var_eps[:, s:s + 1], mean_var[:, s, 1:2], 1.0, EPS,
                                        ALU.mult, ALU.add).then_inc(var_ready, 1)
                pool.wait_ge(var_ready, s + 1)
                nc.gpsimd.tensor_tensor(r_std[:, s:s + 1], var_eps[:, s:s + 1], minus_half[:],
                                        ALU.pow).then_inc(r_std_ready, 1)
                part = r_rows[:, s, POOL_PIECE]
                pool.wait_ge(act_normed, s + 1)
                nc.gpsimd.tensor_tensor(part, part, ln_g_all[:, POOL_PIECE], ALU.mult).then_inc(pool_scaled, 1)
                pool.wait_ge(pool_scaled, s + 1)
                nc.gpsimd.tensor_tensor(part, part, ln_b_all[:, POOL_PIECE], ALU.add).then_inc(pool_rows_ready, 1)

        @block.scalar
        def _(act):
            def split_hi_at(p, j):
                a = j + LEAD
                act.wait_ge(raw_loaded[ring(a)], p * (16 * QUARTERS // RING) + 16 * (a // RING + 1))
                if not (isinstance(p, int) and p == 0 and j == 0):
                    act.wait_ge(quarter_done, p * QUARTERS + j)
                nc.scalar.activation(split_view(a, 0), w_raw[:, ring(a)], ACT.Copy).then_inc(w_hi, 1)

            def xT_split(i):
                act.wait_ge(xT_done, i + 1)
                nc.scalar.activation(xg_split[:, 0, i * XK:(i + 1) * XK], unit_banks(i),
                                     ACT.Copy).then_inc(xT_hi, 1)

            def chunk(p, c):
                act.wait_ge(quarter_done, p * QUARTERS + 4 * (c + 1))
                src = proj[:, 2 * (c % 2):2 * (c % 2) + 2]
                if c == 0:
                    nc.scalar.activation(qT[:, 0], src, ACT.Copy, scale=SCALE).then_inc(chunk_hi, 1)
                elif c == 1:
                    nc.scalar.activation(kT[:, 0], src, ACT.Copy).then_inc(chunk_hi, 1)
                elif c == 2:
                    nc.scalar.activation(v[:, 0], src.rearrange("p b (t e) -> p (b t) e", t=2),
                                         ACT.Copy).then_inc(chunk_hi, 1)
                else:
                    nc.scalar.activation(silu_z, src, ACT.Exp, scale=-1.0)
                    for e in range(2):
                        last = nc.scalar.activation(z_gain[:, e], src[:, e], ACT.Copy, scale=sub_g[:, e:e + 1])
                    last.then_inc(z_moved, 1)

            def exps(p, t):
                act.wait_ge(neg_max_ready, p * ST + t + 1)
                for h in range(2):
                    e = logits[:, h, 0:(t + 1) * P]
                    nc.scalar.activation(e, e, ACT.Exp, bias=neg_max[:, h:h + 1],
                                         accum_out=row_sum[:, h:h + 1]).then_inc(exp_ready, 1)

            def aT_split(p, t):
                if not (isinstance(p, int) and p == 0 and t < 2):
                    act.wait_ge(av_done, p * ST + t - 1)
                act.wait_ge(aT_done, p * ST + t + 1)
                nc.scalar.activation(aT[:, t % 2, 0, 0:(t + 1) * P], turned[:, 0:(t + 1) * P],
                                     ACT.Copy).then_inc(aT_hi, 1)

            def norm(p, t):
                if t == 0 and not (isinstance(p, int) and p == 0):
                    act.wait_ge(g_ready, p * ST)
                act.wait_ge(av_done, p * ST + t + 1)
                nc.scalar.activation(normed[:, t], av, ACT.Square, scale=inv_sum[:, t, 0:1],
                                     accum_out=sq_sum[:, t:t + 1]).then_inc(sq_ready, 1)
                act.wait_ge(o_scale_ready, p * ST + t + 1)
                nc.scalar.activation(normed[:, t], av, ACT.Copy,
                                     scale=o_scale[:, t:t + 1]).then_inc(normed_ready, 1)

            def late_steps(p, j):
                if j == 0:
                    chunk(p, 3)
                if j <= 1:
                    norm(p, j + 2)

            def own_steps(p, j):
                if j in (4, 8, 12):
                    chunk(p, j // 4 - 1)
                if 10 <= j < 14:
                    exps(p, j - 10)
                if j >= 12:
                    aT_split(p, j - 12)
                if j >= 14:
                    norm(p, j - 14)

            def first_split(i):
                act.wait_ge(raw_loaded[i], 16)
                nc.scalar.activation(split_view(i, 0), w_raw[:, i], ACT.Copy).then_inc(w_hi, 1)

            xT_split(0)
            xT_split(1)
            first_split(0)
            for i in range(1, LEAD):
                xT_split(2 * i)
                xT_split(2 * i + 1)
                first_split(i)
            for j in range(QUARTERS):
                split_hi_at(0, j)
                if j == 0:
                    xT_split(XU - 2)
                    xT_split(XU - 1)
                if j == 4:
                    act.wait_ge(lam_sums, 1)
                    nc.scalar.activation(lam_exp[:], att[:, 2, 0:2], ACT.Exp).then_inc(lam_exped, 1)
                    act.wait_ge(sub_ready, 1)
                own_steps(0, j)
            with nc.Fori(1, PAIRS, engines=[mybir.EngineType.Activation], hint_back_edge=True) as p:
                for j in range(QUARTERS):
                    split_hi_at(p, j)
                    late_steps(p - 1, j)
                    own_steps(p, j)

            def g_split_hi(i):
                if i == OQ - 1:
                    act.wait_ge(g_ready, PAIRS * ST)
                else:
                    act.wait_ge(g_ready, (PAIRS - 1) * ST)
                act.wait_ge(quarter_done, TOTAL)
                nc.scalar.activation(xg_split[:, 0, 2 * i:2 * i + 2], g[:, 2 * i:2 * i + 2],
                                     ACT.Copy).then_inc(g_hi, 1)

            act.wait_ge(g_ready, (PAIRS - 1) * ST)
            act.wait_ge(scores_done, PAIRS * ST)
            for i in range(EARLY // 2):
                nc.scalar.activation(g_early[:, 0, 2 * i:2 * i + 2], g[:, 2 * i:2 * i + 2],
                                     ACT.Copy).then_inc(g_hi, 1)

            for c in range(CHUNKS):
                for i in range(OQ):
                    if c == 0 and i in G_STEPS:
                        g_split_hi(G_STEPS[i])
                    for n in out_splits(c, i):
                        act.wait_ge(raw_loaded[ring(n)], 16 * (n // RING + 1))
                        if n < LAST:
                            act.wait_ge(quarter_done, n - LEAD)
                        elif n >= LAST + RING:
                            act.wait_ge(quarter_done, n - LEAD - RING)
                        nc.scalar.activation(out_split_view(n, 0), w_raw[:, ring(n)], ACT.Copy).then_inc(w_hi, 1)
                    if c == 0:
                        late_steps(PAIRS - 1, i)
                    if i == OQ - 2:
                        if c == 0:
                            for n in G_REST:
                                g_split_hi(n)
                            act.wait_ge(silu_ready, PAIRS * ST)
                        else:
                            act.wait_ge(r_ready, ST * c)
                        load_res(act, c)
            for s in range(ST):
                act.wait_ge(shift_ready, s + 1)
                part = r_rows[:, s, POOL_PIECE]
                nc.scalar.activation(part, part, ACT.Identity, scale=r_std[:, s:s + 1],
                                     bias=shift[:, s:s + 1]).then_inc(act_normed, 1)

        @block.vector
        def _(dve):
            nc.vector.memset(table[BUCKETS:BUCKETS + 1, :], MASKED).then_inc(mask_ready, 1)

            def split_lo_at(p, j):
                a = j + LEAD
                dve.wait_ge(w_hi, p * QUARTERS + a + 1)
                nc.vector.tensor_tensor(split_view(a, 1), w_raw[:, ring(a)],
                                        split_view(a, 0).bitcast(F32), ALU.subtract).then_inc(w_ready, 1)

            def xT_split(i):
                dve.wait_ge(xT_hi, i + 1)
                tiles = slice(i * XK, (i + 1) * XK)
                nc.vector.tensor_tensor(xg_split[:, 1, tiles], unit_banks(i), xg_split[:, 0, tiles].bitcast(F32),
                                        ALU.subtract).then_inc(xT_ready, 1)

            def chunk(p, c):
                dve.wait_ge(chunk_hi, p * 3 + c + 1)
                src = proj[:, 2 * (c % 2):2 * (c % 2) + 2]
                if c == 0:
                    nc.vector.scalar_tensor_tensor(qT[:, 1], src, SCALE, qT[:, 0].bitcast(F32),
                                                   ALU.mult, ALU.subtract).then_inc(chunk_moved, 1)
                elif c == 1:
                    nc.vector.tensor_tensor(kT[:, 1], src, kT[:, 0].bitcast(F32),
                                            ALU.subtract).then_inc(chunk_moved, 1)
                else:
                    nc.vector.tensor_tensor(v[:, 1], src.rearrange("p b (t e) -> p (b t) e", t=2),
                                            v[:, 0].bitcast(F32), ALU.subtract).then_inc(chunk_moved, 1)

            def silu(p, t):
                if t == 0:
                    dve.wait_ge(z_moved, p + 1)
                    nc.vector.tensor_scalar(silu_z, silu_z, 1.0, None, ALU.add).then_inc(z_denom, 1)
                    dve.wait_ge(z_denom, p + 1)
                part = silu_z[:, :, t * P:(t + 1) * P]
                nc.vector.reciprocal(part, part).then_inc(z_inv, 1)
                dve.wait_ge(z_inv, p * ST + t + 1)
                nc.vector.tensor_tensor(part, part, z_gain[:, :, t * P:(t + 1) * P],
                                        ALU.mult).then_inc(silu_ready, 1)

            def logits_of(p, t):
                dve.wait_ge(scores_done, p * ST + t + 1)
                if not (isinstance(p, int) and p == 0 and t == 0):
                    dve.wait_ge(a_ready, p * ST + t)
                if t == 0:
                    dve.wait_ge(bias_loaded, p * 16 + 16)
                dve.sem_inc(tile_begun, 1)
                for h in range(2):
                    nc.vector.tensor_tensor_reduce(
                        out=logits[:, h, 0:(t + 1) * P], in0=scores[:, h, 0:(t + 1) * P],
                        in1=bias[:, h, (ST - 1 - t) * P:SEQ], scale=1.0, scalar=LOWEST,
                        op0=ALU.add, op1=ALU.max, accum_out=row_max[:, h:h + 1]).then_inc(max_ready, 1)
                dve.wait_ge(max_ready, (p * ST + t + 1) * 2)
                nc.vector.tensor_scalar(neg_max[:], row_max[:], -1.0, None, ALU.mult).then_inc(neg_max_ready, 1)

            def combine(p, t):
                n = p * ST + t + 1
                if not (isinstance(p, int) and p == 0):
                    dve.wait_ge(normed_ready, n - ST)
                dve.wait_ge(exp_ready, n * 2)
                nc.vector.reciprocal(inv_sum[:, t], row_sum[:]).then_inc(inv_ready, 1)
                dve.wait_ge(inv_ready, n)
                nc.vector.scalar_tensor_tensor(mix[:], row_sum[:, 0:1], neg_lam[:], inv_sum[:, t, 1:2],
                                               ALU.mult, ALU.mult).then_inc(mix_ready, 1)
                if not (isinstance(p, int) and p == 0 and t < 2):
                    dve.wait_ge(aT_done, n - 2)
                dve.wait_ge(mix_ready, n)
                cols = slice(0, (t + 1) * P)
                nc.vector.scalar_tensor_tensor(a_rows[:, t % 2, cols], logits[:, 1, cols], mix[:],
                                               logits[:, 0, cols], ALU.mult, ALU.add).then_inc(a_ready, 1)

            def aT_split(p, t):
                dve.wait_ge(aT_hi, p * ST + t + 1)
                cols = slice(0, (t + 1) * P)
                nc.vector.tensor_tensor(aT[:, t % 2, 1, cols], turned[:, cols],
                                        aT[:, t % 2, 0, cols].bitcast(F32), ALU.subtract).then_inc(aT_ready, 1)

            def norm(p, t):
                dve.wait_ge(rms_ready, p * ST + t + 1)
                nc.vector.tensor_tensor(o_scale[:, t:t + 1], rms[:, t:t + 1], inv_sum[:, t, 0:1],
                                        ALU.mult).then_inc(o_scale_ready, 1)

            def gate(p, t):
                dve.wait_ge(nT_done, p * ST + t + 1)
                dve.wait_ge(silu_ready, p * ST + t + 1)
                turned_n = turned[:, 0:PW].rearrange("p (e s) -> p e s", e=2)
                rows = slice(t * P, (t + 1) * P)
                nc.vector.tensor_tensor(g[:, bass.ds(p * 2, 2), rows], turned_n, silu_z[:, :, rows],
                                        ALU.mult).then_inc(g_ready, 1)

            def late_steps(p, j):
                if j <= 1:
                    norm(p, j + 2)
                if j < 4:
                    silu(p, j)
                if 1 <= j <= 4:
                    gate(p, j - 1)

            def slot(p, j, late):
                if 10 <= j < 14:
                    logits_of(p, j - 10)
                split_lo_at(p, j)
                if late:
                    late_steps(p - 1, j)
                if 10 <= j < 14:
                    combine(p, j - 10)
                if j in (4, 8, 12):
                    chunk(p, j // 4 - 1)
                if j >= 12:
                    aT_split(p, j - 12)
                if j >= 14:
                    norm(p, j - 14)

            def first_split(i):
                dve.wait_ge(w_hi, i + 1)
                nc.vector.tensor_tensor(split_view(i, 1), w_raw[:, i], split_view(i, 0).bitcast(F32),
                                        ALU.subtract).then_inc(w_ready, 1)

            for i in range(LEAD):
                xT_split(2 * i)
                xT_split(2 * i + 1)
                first_split(i)
            for j in range(QUARTERS):
                slot(0, j, False)
                if j == 0:
                    xT_split(XU - 2)
                    xT_split(XU - 1)
                if j == 2:
                    dve.wait_ge(small_loaded, 64)
                    lv = lam_vecs[:].rearrange("p (i j) -> p i j", j=2)
                    nc.vector.tensor_tensor(lam_prod[:], lv[:, :, 0], lv[:, :, 1], ALU.mult).then_inc(lam_step, 1)
                    dve.wait_ge(sub_loaded, 32)
                    nc.vector.tensor_scalar(sub_g[:], sub_raw[:], 1.0 - LAM_INIT, None, ALU.mult).then_inc(sub_ready, 1)
                if j == 4:
                    dve.wait_ge(lam_exped, 1)
                    nc.vector.tensor_tensor(lam_diff[:], lam_exp[:, 1:2], lam_exp[:, 0:1],
                                            ALU.subtract).then_inc(lam_step, 1)
                    dve.wait_ge(lam_step, 2)
                    nc.vector.tensor_scalar(neg_lam[:], lam_diff[:], LAM_INIT, None,
                                            ALU.subtract).then_inc(lam_step, 1)
                    dve.wait_ge(lam_step, 3)
                    dve.wait_ge(bias_line_done, 1)
                    nc.vector.tensor_copy(bias_line.rearrange("h (a b) -> h a b", a=2),
                                          att[0:16, 0:2, 0:BIAS_W // 2]).then_inc(bias_line_ready, 1)
            with nc.Fori(1, PAIRS, engines=[mybir.EngineType.DVE], hint_back_edge=True) as p:
                for j in range(QUARTERS):
                    slot(p, j, True)

            for i in range(EARLY // 2):
                dve.wait_ge(g_hi, i + 1)
                nc.vector.tensor_tensor(g_early[:, 1, 2 * i:2 * i + 2], g[:, 2 * i:2 * i + 2],
                                        g_early[:, 0, 2 * i:2 * i + 2].bitcast(F32),
                                        ALU.subtract).then_inc(g_split, 1)

            def g_split_lo(i):
                dve.wait_ge(g_hi, EARLY // 2 + G_ORDER.index(i) + 1)
                tiles = slice(2 * i, 2 * i + 2)
                nc.vector.tensor_tensor(xg_split[:, 1, tiles], g[:, tiles], xg_split[:, 0, tiles].bitcast(F32),
                                        ALU.subtract).then_inc(g_split, 1)

            def out_banks(c):
                return proj if c % 2 == 0 else att

            def residual(c, s):
                dve.wait_ge(res_loaded, 16 * (c + 1))
                nc.vector.scalar_tensor_tensor(r_rows[:, s, c * NC:(c + 1) * NC], x_res[:, s], ALPHA,
                                               out_banks(c)[:, s], ALU.mult, ALU.add).then_inc(r_ready, 1)
                dve.wait_ge(r_ready, ST * c + s + 1)
                nc.vector.bn_stats(stats[:, s, c], r_rows[:, s, c * NC:(c + 1) * NC]).then_inc(stats_ready, 1)

            for c in range(CHUNKS):
                for i in range(OQ):
                    if c == 0 and i in G_STEPS:
                        g_split_lo(G_STEPS[i])
                    for n in out_splits(c, i):
                        dve.wait_ge(w_hi, n + 1)
                        nc.vector.tensor_tensor(out_split_view(n, 1), w_raw[:, ring(n)],
                                                out_split_view(n, 0).bitcast(F32),
                                                ALU.subtract).then_inc(w_ready, 1)
                    if c == 0:
                        late_steps(PAIRS - 1, i)
                        if i == OQ - 2:
                            for n in G_REST:
                                g_split_lo(n)
                    elif i < ST:
                        if i == 0:
                            dve.wait_ge(quarter_done, TOTAL + OQ * c)
                            if c == 1:
                                dve.wait_ge(g_split, len(G_ORDER) + EARLY // 2)
                        residual(c - 1, i)
            for s in range(ST):
                c = CHUNKS - 1
                dve.wait_ge(tile_done, s + 1)
                residual(c, s)
                dve.wait_ge(stats_ready, ST * c + s + 1)
                nc.vector.bn_aggr(mean_var[:, s], stats[:, s].rearrange("p c k -> p (c k)")).then_inc(mv_ready, 1)
                dve.wait_ge(mv_ready, s + 1)
                if s == 0:
                    dve.wait_ge(ln_loaded, 32)
                for cols in VECTOR_PIECES:
                    nc.vector.scalar_tensor_tensor(r_rows[:, s, cols], r_rows[:, s, cols], mean_var[:, s, 0:1],
                                                   ln_g_all[:, cols], ALU.subtract, ALU.mult).then_inc(centred, 1)
                    if cols == VECTOR_PIECES[0]:
                        dve.wait_ge(r_std_ready, s + 1)
                        nc.vector.scalar_tensor_tensor(shift[:, s:s + 1], mean_var[:, s, 0:1], -1.0,
                                                       r_std[:, s:s + 1], ALU.mult, ALU.mult
                                                       ).then_inc(shift_ready, 1)
                for i, cols in enumerate(VECTOR_PIECES):
                    dve.wait_ge(centred, len(VECTOR_PIECES) * s + i + 1)
                    nc.vector.scalar_tensor_tensor(r_rows[:, s, cols], r_rows[:, s, cols], r_std[:, s:s + 1],
                                                   ln_b_all[:, cols], ALU.mult, ALU.add).then_inc(rows_ready, 1)

        @block.tensor
        def _(pe):
            def mm(dst, lhsT, rhs, start, stop):
                return nc.tensor.matmul(dst, lhsT, rhs, start=start, stop=stop, skip_group_check=True)

            def small_products():
                pe.wait_ge(table_loaded, 32)
                pe.wait_ge(mask_ready, 1)
                for i in range(2):
                    last = nc.tensor.matmul(att[0:16, i, 0:BIAS_W // 2], table[:],
                                            onehot[:, i * BIAS_W // 2:(i + 1) * BIAS_W // 2],
                                            start=True, stop=True)
                last.then_inc(bias_line_done, 1)
                pe.wait_ge(lam_step, 1)
                nc.tensor.matmul(att[:, 2, 0:2], ones[:], lam_prod[:], start=True, stop=True).then_inc(lam_sums, 1)

            def turn_x(i):
                pe.wait_ge(x_loaded[i], 16)
                if i >= 3:
                    pe.wait_ge(xT_ready, i - 2)
                for k in range(XK):
                    for s in range(ST):
                        col = (XK * i + k) * P
                        last = nc.tensor.transpose(unit_banks(i)[:, k, s * P:(s + 1) * P],
                                                   x_rows[:, s, col:col + P], ident[:])
                last.then_inc(xT_done, 1)

            def quarter(p, j):
                c, part = j // 4, j % 4
                pe.wait_ge(w_ready, p * QUARTERS + j + 1)
                if part == 0 and c == 1:
                    if not (isinstance(p, int) and p == 0):
                        pe.wait_ge(z_moved, p)
                elif part == 0 and not (isinstance(p, int) and p == 0 and c == 0):
                    pe.wait_ge(chunk_moved, p * 3 + (c // 2) + (c // 3))
                w = [split_view(j, l).rearrange("p (k n) -> p k n", k=QK) for l in range(2)]
                bank = 2 * (c % 2)
                for kk in range(QK):
                    k = part * QK + kk
                    x_hi, x_lo = xg_split[:, 0, k], xg_split[:, 1, k]
                    first, final = k == 0, k == KT - 1
                    if c == 2:
                        for s in range(ST):
                            rows = slice(s * P, (s + 1) * P)
                            dst = proj[:, bank + s // 2, (s % 2) * PW:(s % 2 + 1) * PW]
                            mm(dst, x_hi[:, rows], w[0][:, kk], first and s % 2 == 0, False)
                            mm(dst, x_hi[:, rows], w[1][:, kk], False, False)
                            last = mm(dst, x_lo[:, rows], w[0][:, kk], False, final and s % 2 == 1)
                    else:
                        for e in range(2):
                            cols = slice(e * P, (e + 1) * P)
                            dst = proj[:, bank + e]
                            mm(dst, w[0][:, kk, cols], x_hi, first, False)
                            mm(dst, w[0][:, kk, cols], x_lo, False, False)
                            last = mm(dst, w[1][:, kk, cols], x_hi, False, final)
                last.then_inc(quarter_done, 1)

            def scores_of(p, t):
                if t == 0:
                    pe.wait_ge(chunk_moved, p * 3 + 2)
                if t:
                    pe.wait_ge(max_ready, p * (2 * ST) + 2 * t)
                n = max(t + 1, 2) * P
                rows = slice(t * P, (t + 1) * P)
                for h in range(2):
                    dst = scores[:, h, 0:n]
                    mm(dst, qT[:, 0, h, rows], kT[:, 0, h, 0:n], True, False)
                    mm(dst, qT[:, 0, h, rows], kT[:, 1, h, 0:n], False, False)
                    last = mm(dst, qT[:, 1, h, rows], kT[:, 0, h, 0:n], False, True)
                last.then_inc(scores_done, 1)

            def turn_a(p, t):
                pe.wait_ge(a_ready, p * ST + t + 1)
                if t == 0:
                    if not (isinstance(p, int) and p == 0):
                        pe.wait_ge(g_ready, p * ST)
                else:
                    pe.wait_ge(aT_ready, p * ST + t)
                for kt in range(t + 1):
                    cols = slice(kt * P, (kt + 1) * P)
                    last = nc.tensor.transpose(turned[:, cols], a_rows[:, t % 2, cols], ident[:])
                last.then_inc(aT_done, 1)

            def weigh_v(p, t):
                pe.wait_ge(aT_ready, p * ST + t + 1)
                if t == 0:
                    pe.wait_ge(chunk_moved, p * 3 + 3)
                if not (isinstance(p, int) and p == 0 and t == 0):
                    pe.wait_ge(normed_ready, p * ST + t)
                dst = av
                for kt in range(t + 1):
                    cols = slice(kt * P, (kt + 1) * P)
                    a_hi, a_lo = aT[:, t % 2, 0, cols], aT[:, t % 2, 1, cols]
                    mm(dst, a_hi, v[:, 0, kt], kt == 0, False)
                    mm(dst, a_hi, v[:, 1, kt], False, False)
                    last = mm(dst, a_lo, v[:, 0, kt], False, kt == t)
                last.then_inc(av_done, 1)

            def turn_normed(p, t):
                pe.wait_ge(normed_ready, p * ST + t + 1)
                if t == 0:
                    pe.wait_ge(aT_ready, p * ST + ST)
                else:
                    pe.wait_ge(g_ready, p * ST + t)
                for e in range(2):
                    last = nc.tensor.transpose(turned[:, e * P:(e + 1) * P],
                                               normed[:, t, e * P:(e + 1) * P], ident[:])
                last.then_inc(nT_done, 1)

            def late_inserts(p, j):
                if j == 0:
                    weigh_v(p, 3)
                if j < 4:
                    turn_normed(p, j)

            def own_inserts(p, j):
                if 9 <= j < 13:
                    scores_of(p, j - 9)
                if 11 <= j < 15:
                    turn_a(p, j - 11)
                if 13 <= j:
                    weigh_v(p, j - 13)

            pe.wait_ge(consts_ready, 3)
            for i in range(4):
                turn_x(i)
            for j in range(QUARTERS):
                if j < 4:
                    pe.wait_ge(xT_ready, 2 * j + 2)
                quarter(0, j)
                if j < 2:
                    turn_x(2 * j + 4)
                    turn_x(2 * j + 5)
                if j == 3:
                    small_products()
                if j == 8:
                    pe.wait_ge(bias_line_ready, 1)
                own_inserts(0, j)
            with nc.Fori(1, PAIRS, engines=[mybir.EngineType.PE], hint_back_edge=True) as p:
                for j in range(QUARTERS):
                    quarter(p, j)
                    late_inserts(p - 1, j)
                    own_inserts(p, j)

            def out_product(c, i, s, w_hi_part, w_lo_part, first, final):
                dst = (proj if c % 2 == 0 else att)[:, s]
                for kk in range(OK):
                    k = i * OK + kk
                    rows = slice(s * P, (s + 1) * P)
                    src = g_early if c == 0 and k < EARLY else xg_split
                    g_hi_part, g_lo_part = src[:, 0, k, rows], src[:, 1, k, rows]
                    wh = w_hi_part.rearrange("p (k n) -> p k n", k=OK)[:, kk]
                    wl = w_lo_part.rearrange("p (k n) -> p k n", k=OK)[:, kk]
                    mm(dst, g_hi_part, wh, first and kk == 0, False)
                    mm(dst, g_hi_part, wl, False, False)
                    last = mm(dst, g_lo_part, wh, False, final and kk == OK - 1)
                return last

            for c in range(CHUNKS - 1):
                for i in range(OQ):
                    n = TOTAL + c * OQ + i
                    pe.wait_ge(w_ready, n + 1)
                    if c == 0:
                        pe.wait_ge(g_split, i + 1)
                    elif i == 0 and c == 1:
                        pe.wait_ge(g_split, len(G_ORDER) + EARLY // 2)
                    elif i == 0:
                        pe.wait_ge(r_ready, ST)
                    for s in range(ST):
                        if c == 0 and i == 0 and s == 2:
                            pe.wait_ge(z_moved, PAIRS)
                        last = out_product(c, i, s, split_view(n, 0), split_view(n, 1), i == 0, i == OQ - 1)
                    last.then_inc(quarter_done, 1)
                    if c == 0:
                        late_inserts(PAIRS - 1, i)
            pe.wait_ge(r_ready, 2 * ST)
            for s in range(ST):
                for i in range(OQ):
                    n = LAST + i
                    if s == 0:
                        pe.wait_ge(w_ready, n + 1)
                    last = out_product(CHUNKS - 1, i, s, out_split_view(n, 0), out_split_view(n, 1),
                                       i == 0, i == OQ - 1)
                last.then_inc(tile_done, 1)


LAST = PAIRS * QUARTERS + (CHUNKS - 1) * OQ

G_STEPS = {i: i + 2 for i in range(OQ - 3)}
G_REST = [OQ - 1, 0, 1]
G_ORDER = [*G_STEPS.values(), *G_REST]

VECTOR_PIECES = [slice(0, D // 2), slice(D // 2, 3 * D // 4)]
POOL_PIECE = slice(3 * D // 4, D)

_INS = ["x", "rel_bias", "w_in_0", "lam_q1_0", "lam_k1_0", "lam_q2_0", "lam_k2_0", "subln_g_0", "w_out_0",
        "ln_g_0", "ln_b_0"]


def _bucket_onehot():
    import numpy as np
    dist = SEQ - 1 - np.arange(BIAS_W)
    n = np.maximum(dist, 1).astype(np.float32)
    exact = BUCKETS // 2
    large = exact + (np.log(n / np.float32(exact)) / np.float32(math.log(128 / exact))
                     * np.float32(BUCKETS - exact)).astype(np.int32)
    bucket = np.where(dist < exact, dist, np.minimum(large, BUCKETS - 1))
    bucket = np.where(dist < 0, BUCKETS, bucket)
    return (np.arange(BUCKETS + 1)[:, None] == bucket[None, :]).astype(np.float32)


def kernel(**inputs):
    import numpy as _np
    import concourse.bacc as _bacc
    from concourse import mybir as _mybir
    from concourse.bass_utils import run_bass_kernel_spmd as _run

    nc = _bacc.Bacc("TRN2", target_bir_lowering=False, num_devices=1)
    arrays, args = {}, []
    for name in _INS:
        a = _np.ascontiguousarray(inputs[name])
        arrays[f"in_{name}_dram"] = a
        args.append(nc.dram_tensor(f"in_{name}_dram", a.shape, _mybir.dt.from_np(a.dtype), kind="ExternalInput").ap())
    onehot = _bucket_onehot()
    arrays["bucket_onehot_dram"] = onehot
    args.append(nc.dram_tensor("bucket_onehot_dram", onehot.shape, _mybir.dt.from_np(onehot.dtype),
                               kind="ExternalInput").ap())
    args.append(nc.dram_tensor("out_dram", (1, SEQ, D), _mybir.dt.float32, kind="ExternalOutput").ap())
    diff_layer(nc, *args)
    r = _run(nc, [arrays], core_ids=[0])
    return r.results[0]["out_dram"]
```
